# Optimizing a Trainium2 kernel written in Bass

```python
import math
import jax, jax.numpy as jnp
from jax import lax
import numpy as np

D_MODEL = 1024
BATCH = 1
SEQ = 512
DEPTH = 1

D_ATTN = 512
HEAD_DIM = 64
N_ATTN_HEADS = D_ATTN // HEAD_DIM
D_CONV = D_MODEL - D_ATTN
N_CONV_GROUPS = D_CONV // 64
CONV_WIDTH = 3
Q_BLOCK = 128
D_IN_PROJ = 3 * D_ATTN + 3 * D_CONV

N_GROUPS = 4
EXPERTS_PER_GROUP = 8
N_EXPERTS = N_GROUPS * EXPERTS_PER_GROUP
TOP_K_IN_GROUP = 2
D_EXPERT = 256

DEEPNORM_ALPHA = (2.0 * DEPTH) ** 0.25
DEEPNORM_BETA = (8.0 * DEPTH) ** -0.25
N_ADA = 6
LN_EPS = 1e-5

kernel_name = "hybrid_stickbreak_shortconv_hmoe_deepnorm_adaln"

def _layer_norm(x, g, b):
    xf = x.astype(jnp.float32)
    mu = jnp.mean(xf, axis=-1, keepdims=True)
    var = jnp.mean(jnp.square(xf - mu), axis=-1, keepdims=True)
    y = (xf - mu) * lax.rsqrt(var + LN_EPS)
    return (y * g.astype(jnp.float32) + b.astype(jnp.float32)).astype(x.dtype)

def _stick_breaking_attention(q, k, v):
    seq = q.shape[2]
    scale = HEAD_DIM ** -0.5
    outs = []
    for blk in range(seq // Q_BLOCK):
        start = blk * Q_BLOCK
        end = start + Q_BLOCK
        qb = q[:, :, start:end].astype(jnp.float32)
        kb = k[:, :, :end].astype(jnp.float32)
        vb = v[:, :, :end]
        z = jnp.einsum('bhqd,bhkd->bhqk', qb, kb) * scale
        t_pos = start + jnp.arange(Q_BLOCK)
        s_pos = jnp.arange(end)
        causal = s_pos[None, :] < t_pos[:, None]
        log_stay = jnp.where(causal, jax.nn.log_sigmoid(-z), 0.0)
        log_stay_after = lax.cumsum(log_stay, axis=3, reverse=True) - log_stay
        a = jnp.where(causal, jnp.exp(jax.nn.log_sigmoid(z) + log_stay_after), 0.0)
        outs.append(jnp.einsum('bhqk,bhkd->bhqd', a.astype(vb.dtype), vb))
    return jnp.concatenate(outs, axis=2)

def _causal_depthwise_conv(u, w):
    seq = u.shape[1]
    up = jnp.pad(u, ((0, 0), (CONV_WIDTH - 1, 0), (0, 0)))
    return sum(w[kk][None, None, :] * up[:, kk:kk + seq] for kk in range(CONV_WIDTH))

def _hierarchical_moe(h, w_rg, b_rg, w_re, b_re, w_gate, w_up, w_down):
    t = h.shape[0]
    hf = h.astype(jnp.float32)
    group_logits = hf @ w_rg.astype(jnp.float32) + b_rg.astype(jnp.float32)
    group_probs = jax.nn.softmax(group_logits, axis=-1)
    g_prob, g_idx = lax.top_k(group_probs, 1)
    exp_logits = (hf @ w_re.astype(jnp.float32) + b_re.astype(jnp.float32))
    exp_logits = exp_logits.reshape(t, N_GROUPS, EXPERTS_PER_GROUP)
    sel_logits = jnp.take_along_axis(exp_logits, g_idx[:, :, None], axis=1)[:, 0]
    sel_probs = jax.nn.softmax(sel_logits, axis=-1)
    top_p, top_i = lax.top_k(sel_probs, TOP_K_IN_GROUP)
    top_w = top_p / jnp.sum(top_p, axis=-1, keepdims=True) * g_prob
    in_group = jnp.sum(jax.nn.one_hot(top_i, EXPERTS_PER_GROUP, dtype=jnp.float32)
                       * top_w[:, :, None], axis=1)
    combine = jax.nn.one_hot(g_idx[:, 0], N_GROUPS, dtype=jnp.float32)[:, :, None] \
        * in_group[:, None, :]
    combine = combine.astype(h.dtype)
    w_gate = w_gate.reshape(N_GROUPS, EXPERTS_PER_GROUP, D_MODEL, D_EXPERT)
    w_up = w_up.reshape(N_GROUPS, EXPERTS_PER_GROUP, D_MODEL, D_EXPERT)
    w_down = w_down.reshape(N_GROUPS, EXPERTS_PER_GROUP, D_EXPERT, D_MODEL)
    y = jnp.zeros_like(h)
    for g in range(N_GROUPS):
        hid = jax.nn.silu(jnp.einsum('td,edf->tef', h, w_gate[g])) \
            * jnp.einsum('td,edf->tef', h, w_up[g])
        y = y + jnp.einsum('tef,te,efd->td', hid, combine[:, g], w_down[g])
    return y

def setup_inputs(seed: int = 0) -> dict:
    key = jax.random.key(seed)
    ks = jax.random.split(key, 20)
    f32 = jnp.float32
    d = D_MODEL
    x = jax.random.normal(ks[0], (BATCH, SEQ, d), f32)
    c = jax.random.normal(ks[1], (BATCH, d), f32)
    w_ada = jax.random.normal(ks[2], (DEPTH, d, N_ADA * d), f32) * (0.1 * d ** -0.5)
    ada_noise = 0.01 * jax.random.normal(ks[3], (DEPTH, N_ADA, d), f32)
    gate_bias = jnp.array([0.0, 0.0, 1.0, 0.0, 0.0, 1.0], f32)[None, :, None]
    b_ada = (ada_noise + gate_bias).reshape(DEPTH, N_ADA * d)
    w_in = jax.random.normal(ks[4], (DEPTH, d, D_IN_PROJ), f32) * d ** -0.5
    conv_w = jax.random.normal(ks[5], (DEPTH, CONV_WIDTH, D_CONV), f32) * CONV_WIDTH ** -0.5
    w_out = jax.random.normal(ks[6], (DEPTH, d, d), f32) * (d ** -0.5 * DEEPNORM_BETA)
    ln1_g = 1.0 + 0.01 * jax.random.normal(ks[7], (DEPTH, d), f32)
    ln1_b = 0.01 * jax.random.normal(ks[8], (DEPTH, d), f32)
    w_router_group = jax.random.normal(ks[9], (DEPTH, d, N_GROUPS), f32) * d ** -0.5
    b_router_group = 0.01 * jax.random.normal(ks[10], (DEPTH, N_GROUPS), f32)
    w_router_expert = jax.random.normal(ks[11], (DEPTH, d, N_EXPERTS), f32) * d ** -0.5
    b_router_expert = 0.01 * jax.random.normal(ks[12], (DEPTH, N_EXPERTS), f32)
    w_gate = jax.random.normal(ks[13], (DEPTH, N_EXPERTS, d, D_EXPERT), f32) * d ** -0.5
    w_up = jax.random.normal(ks[14], (DEPTH, N_EXPERTS, d, D_EXPERT), f32) * d ** -0.5
    w_down = jax.random.normal(ks[15], (DEPTH, N_EXPERTS, D_EXPERT, d), f32) \
        * (D_EXPERT ** -0.5 * DEEPNORM_BETA)
    ln2_g = 1.0 + 0.01 * jax.random.normal(ks[16], (DEPTH, d), f32)
    ln2_b = 0.01 * jax.random.normal(ks[17], (DEPTH, d), f32)
    return {"x": x, "c": c, "w_ada": w_ada, "b_ada": b_ada, "w_in": w_in,
            "conv_w": conv_w, "w_out": w_out, "ln1_g": ln1_g, "ln1_b": ln1_b,
            "w_router_group": w_router_group, "b_router_group": b_router_group,
            "w_router_expert": w_router_expert, "b_router_expert": b_router_expert,
            "w_gate": w_gate, "w_up": w_up, "w_down": w_down,
            "ln2_g": ln2_g, "ln2_b": ln2_b}

def reference(x, c, w_ada, b_ada, w_in, conv_w, w_out, ln1_g, ln1_b,
              w_router_group, b_router_group, w_router_expert, b_router_expert,
              w_gate, w_up, w_down, ln2_g, ln2_b):
    bsz, seq, d = x.shape
    for l in range(DEPTH):
        ada = (jax.nn.silu(c) @ w_ada[l] + b_ada[l]).reshape(bsz, N_ADA, d)
        shift1, scale1, gate1, shift2, scale2, gate2 = [ada[:, i][:, None, :] for i in range(N_ADA)]

        h = x * (1.0 + scale1) + shift1
        proj = h @ w_in[l]
        q, k, v, cb, cc, cx = jnp.split(
            proj, np.cumsum([D_ATTN, D_ATTN, D_ATTN, D_CONV, D_CONV]).tolist(), axis=-1)
        to_heads = lambda t: t.reshape(bsz, seq, N_ATTN_HEADS, HEAD_DIM).transpose(0, 2, 1, 3)
        attn = _stick_breaking_attention(to_heads(q), to_heads(k), to_heads(v))
        attn = attn.transpose(0, 2, 1, 3).reshape(bsz, seq, D_ATTN)
        conv = cb * _causal_depthwise_conv(cc * cx, conv_w[l])
        mix = jnp.concatenate([attn, conv], axis=-1) @ w_out[l]
        x = _layer_norm(DEEPNORM_ALPHA * x + gate1 * mix, ln1_g[l], ln1_b[l])

        h2 = (x * (1.0 + scale2) + shift2).reshape(bsz * seq, d)
        moe = _hierarchical_moe(h2, w_router_group[l], b_router_group[l],
                                w_router_expert[l], b_router_expert[l],
                                w_gate[l], w_up[l], w_down[l]).reshape(bsz, seq, d)
        x = _layer_norm(DEEPNORM_ALPHA * x + gate2 * moe, ln2_g[l], ln2_b[l])
    return x


_drawn_inputs = setup_inputs


def setup_inputs(seed=0):
    import zlib

    import numpy as np

    out = dict(_drawn_inputs(seed))
    spreads = {}
    factors = {'ln1_g': 4.21,
     'ln1_b': 4.394,
     'b_router_group': 8.0,
     'b_router_expert': 7.73,
     'ln2_g': 5.714,
     'ln2_b': 5.744}
    for name, (base, spread) in spreads.items():
        noise = np.random.default_rng([zlib.crc32(name.encode()), seed]).standard_normal(out[name].shape)
        drawn = base * np.exp(spread * noise) if base else spread * noise
        out[name] = __import__('jax').numpy.asarray(drawn.astype(out[name].dtype))
    for name, factor in factors.items():
        out[name] = (out[name] * factor).astype(out[name].dtype)
    return out
```

```python
from contextlib import ExitStack

import concourse.bass as bass
from concourse import mybir

F32 = mybir.dt.float32
BF16 = mybir.dt.bfloat16
I32 = mybir.dt.int32
ALU = mybir.AluOpType
ACT = mybir.ActivationFunctionType
AX = mybir.AxisListType.X

P = 128
D = 1024
T = 512
KC = D // P
TC = T // P
DA = 512
HD = 64
NH = DA // HD
NF = DA // P
CONV_W = 3
NG, EPG = 4, 8
NE = NG * EPG
FE = 256
NADA = 6
EPS = 1e-5
ALPHA = 2.0 ** 0.25
BIG = 1e30

SLOTS = 64
HALF = NE // 2
NPAIR = NE // 2
NOVB = 16
NOVP = NOVB // 2
NCOL = NPAIR + NOVP
RING = 3
LAST0 = (NPAIR + RING - 1) // RING
SKIP = 4096

CW = 256
NSTG = 4
NADACH = NADA * D // CW
ADA1 = 2 * D // CW
ADA_PE = 5
ADA_FIRST = [0, 5, 1, 2, 6, 3, 4, 7]

Q, K_, V_, CB, CC, CX = (n * DA // CW for n in range(6))
W_ORDER = [Q, Q + 1, K_, K_ + 1, V_, V_ + 1, CC, CX, CB, CC + 1, CX + 1, CB + 1]


def stage_order():
    seq = [("ada", i) for i in ADA_FIRST]
    rest = list(range(ADA1, NADACH))
    for n, w in enumerate(W_ORDER):
        seq.append(("w", w))
        take = 2 if n < 6 else 1
        seq += [("ada", rest.pop(0)) for _ in range(min(take, len(rest)))]
    return seq


SEQ = stage_order()
CONV_OUT = [(kind, f) for g in range(2) for kind in ("cc", "cx", "cb") for f in (2 * g, 2 * g + 1)]
CONV_AT = [0, 2, 3, 5, 6, 8, 9, 11, 12]
NOWHERE = 1024
OVT = 256
DIAG, OFF0, OFF2, OFF1, ZW = 0, 512, 896, 1024, 1280


def layer_kernel(nc, x, c, w_ada, b_ada, w_in, conv_w, w_out, ln1_g, ln1_b, w_router_group,
                 b_router_group, w_router_expert, b_router_expert, w_gate, w_up, w_down,
                 ln2_g, ln2_b, out):
    ctx = ExitStack()
    with ctx:
        base = (nc.sbuf_base + 31) // 32 * 32

        def at(name, shape, off, dt=F32):
            return nc.alloc_sbuf_tensor_at(name, shape, dt, offset=base + off)

        def sem(name):
            return ctx.enter_context(nc.semaphore(name))

        KB = 1024
        EXP_B = 24 * KB
        w_gu = [[at(f"w_gu{u}{e}", [P, 2, KC, FE], (2 * u + e) * EXP_B) for e in range(2)] for u in range(RING)]
        w_dn = [[at(f"w_dn{u}{e}", [P, 2, D], (2 * u + e) * EXP_B + 16 * KB) for e in range(2)] for u in range(RING)]
        PAIR1, PAIR2, REST = 48 * KB, 96 * KB, 144 * KB
        stage = [at(f"stage{n}", [P, KC, CW], n * 8 * KB) for n in range(NSTG)]
        acc_rows = at("acc_rows", [P, 4 * D], 32 * KB)
        qz = at("qz", [P, NH, T], PAIR1)
        kT = at("kT", [P, NF, T], PAIR1 + 16 * KB)
        v = at("v", [P, TC, DA], PAIR1 + 24 * KB)
        expo = [at(f"expo{n}", [P, ZW], o) for n, o in enumerate(
            (PAIR1 + 32 * KB, PAIR1 + 37 * KB, REST + 48 * KB, PAIR1 + 42 * KB))]
        acc_cols = at("acc_cols", [P, ADA_PE * CW], PAIR1 + 32 * KB)
        conv_rows = at("conv_rows", [P, P], PAIR1 + 42 * KB)
        suffix = [at(f"suffix{n}", [P, 3 * P], REST + 53 * KB + n * 1536) for n in range(2)]
        u_conv = at("u_conv", [P, T], PAIR2 + 46 * KB)
        b24 = at("b24", [P, CW], PAIR1 + 47 * KB)
        wo = at("wo", [P, KC, D], PAIR2)
        softp = [at(f"softp{n}", [P, ZW], PAIR2 + 32 * KB + n * 5 * KB) for n in range(2)]
        cc_sb = [at(f"cc_sb{n}", [P, T], PAIR2 + 42 * KB + n * 2 * KB) for n in range(2)]
        h2nat = at("h2nat", [P, D], PAIR2 + 32 * KB)
        h2p = [at(f"h2p{n}", [P, D], PAIR2 + (36 + 4 * n) * KB) for n in range(2)]
        h2T = at("h2T", [P, KC, P], PAIR2 + 44 * KB)
        xs = at("xs", [P, TC, D], REST)
        hT = at("hT", [P, KC, T], REST + 16 * KB)
        rows = [at(f"rows_{n}", [P, D], REST + (16 + 4 * k) * KB) for k, n in enumerate(("gate1", "a2", "b2", "gate2"))]
        gate1r, a2r, b2r, gate2r = rows
        ysb = [at(f"ysb{n}", [P, D], REST + (16 + 4 * n) * KB) for n in range(RING)]
        mixT = at("mixT", [P, KC, T], REST + 32 * KB)
        xT = [at(f"xT{n}", [P, KC, P], REST + (32 + 4 * n) * KB) for n in range(RING)]
        xg = [at(f"xg{n}", [P, D], REST + (44 + 4 * n) * KB) for n in range(RING)]
        g1r = at("g1r", [P, D], REST + 48 * KB)
        b1r = at("b1r", [P, D], REST + 52 * KB)
        y_tok = [at(f"y_tok{i}", [P, 2, D], PAIR1 + i * 8 * KB) for i in range(TC)]
        g2r = at("g2r", [P, D], PAIR2)
        bb2r = at("bb2r", [P, D], PAIR2 + 4 * KB)

        small = [REST + 56 * KB]

        def sm(name, shape, dt=F32):
            n = 1
            for s in shape[1:]:
                n *= s
            o = small[0]
            small[0] += (n * (2 if dt == BF16 else 4) + 31) // 32 * 32
            return at(name, shape, o, dt)

        ident = sm("ident", [P, P])
        tri_neg = sm("tri_neg", [P, P])
        neg_ones = sm("neg_ones", [P, P])
        ones = sm("ones", [P, P])
        before = sm("before", [P, P], BF16)
        ones_b = sm("ones_b", [P, P], BF16)
        iota = sm("iota", [P, P])
        silu_sb = [sm(f"silu_sb{n}", [P, P]) for n in range(2)]
        hid = [sm(f"hid{n}", [P, P]) for n in range(2)]
        slot_tok = sm("slot_tok", [P, NCOL], I32)
        slot_row = sm("slot_row", [P, NCOL], I32)
        flag = sm("flag", [P, 1], I32)
        blk_exp = sm("blk_exp", [P, NOVB], I32)
        wk = sm("wk", [P, 2, TC])
        mh = sm("mh", [P, 1])
        colsb = sm("colsb", [P, 2 * KC])
        cwT = sm("cwT", [P, CONV_W * NF])
        csil = sm("csil", [P, 4, KC])
        bn = sm("bn", [P, 2, 6])
        mv = sm("mv", [P, 2 * TC, 2])
        var_e = sm("var_e", [P, 2 * TC])
        rstd = sm("rstd", [P, 2 * TC])
        neg_mean = sm("neg_mean", [P, TC + 2])
        shift_n = sm("shift_n", [P, TC + 2])
        w_r = sm("w_r", [P, KC, NG + NE])
        b_r = sm("b_r", [P, NG + NE])
        lowv = sm("lowv", [P, 2, TC])
        highv = sm("highv", [P, 2, TC])
        assert base + small[0] <= nc.sbuf_usable_end, (small[0], nc.sbuf_usable_end - base)
        hidT = [at("hidT0", [P, P], REST + 56 * KB + 512), at("hidT1", [P, P], REST + 56 * KB + 1024)]

        rt = [REST + 20 * KB]

        def rtm(name, shape, dt=F32):
            n = 1
            for s in shape[1:]:
                n *= s
            o = rt[0]
            rt[0] += n * (2 if dt == BF16 else 4)
            assert rt[0] <= REST + 28 * KB
            return at(name, shape, o, dt)

        lg = rtm("lg", [P, TC, NG + NE])
        lem = rtm("lem", [P, TC, NE])
        t32 = rtm("t32", [P, TC, NE])
        oh = rtm("oh", [P, 2, TC, NE])
        rowhot = rtm("rowhot", [P, 8, P], BF16)
        oh_t = at("oh_t", [P, 2, TC, NE], rt[0] - 2 * 8 * P)
        colhot = rtm("colhot", [P, 8, 3, NPAIR], BF16)
        colhot_ov = rtm("colhot_ov", [P, 8, 3, NOVP], BF16)
        mb = rtm("mb", [P, TC, NE], BF16)
        cum = [rtm(f"cum{n}", [P, 16 + NE]) for n in range(2)]
        g4 = rtm("g4", [P, 3, TC, NG])
        sc = rtm("sc", [P, 20, 2, TC])

        ps = ctx.enter_context(nc.psum_tensor("ps", [P, 8, 512], F32))
        flat = ps.rearrange("p b n -> p (b n)")

        h2_dram = nc.dram_tensor("h2_dram", [T, D], F32, kind="Internal").ap()
        y_dram = nc.dram_tensor("y_dram", [2 * T, D], F32, kind="Internal").ap()

        ld_c, ld_b24, ld_cw, ld_x, ld_g1, ld_b1, ld_wr, ld_br, ld_wo, ld_g2 = (
            sem(n) for n in ("ld_c", "ld_b24", "ld_cw", "ld_x", "ld_g1", "ld_b1", "ld_wr", "ld_br", "ld_wo", "ld_g2"))
        ld_stage = [sem(f"ld_stage{n}") for n in range(NSTG)]
        ld_gu = [[sem(f"ld_gu{u}{e}") for e in range(2)] for u in range(RING)]
        ld_dn = [[sem(f"ld_dn{u}{e}") for e in range(2)] for u in range(RING)]
        ld_y = [[sem(f"ld_y{i}{k}") for k in range(2)] for i in range(TC)]
        st_h2 = [sem(f"st_h2{n}") for n in range(2)]
        gathered = [sem(f"gathered{u}") for u in range(RING)]
        ov_gathered, xg_clear = sem("ov_gathered"), sem("xg_clear")
        scattered = [sem(f"scattered{u}") for u in range(RING)]
        ov_ld = sem("ov_ld")
        st_out = sem("st_out")
        fills, consts = sem("fills"), sem("consts")
        exp_c, cs_ready = sem("exp_c"), sem("cs_ready")
        ada_done, ada_pe_done, cols_done = sem("ada_done"), sem("ada_pe_done"), sem("cols_done")
        cw_done, cw_ev = sem("cw_done"), sem("cw_ev")
        xt_done, xt_ev, ht_done = sem("xt_done"), sem("xt_ev"), sem("ht_done")
        proj_done, proj_ev = sem("proj_done"), sem("proj_ev")
        conv_done, conv_ev = sem("conv_done"), sem("conv_ev")
        z_done, abs_done, exp_done, ln_done = sem("z_done"), sem("abs_done"), sem("exp_done"), sem("ln_done")
        sp_done, sp_masked, suf_done, tri_done = sem("sp_done"), sem("sp_masked"), sem("suf_done"), sem("tri_done")
        prob_done, prob_masked, av_done, av_ev = sem("prob_done"), sem("prob_masked"), sem("av_done"), sem("av_ev")
        row_done, row_ev, rows_ready, scaled = sem("row_done"), sem("row_ev"), sem("rows_ready"), sem("scaled")
        out_done, mixg_done, var_done, rstd_done = sem("out_done"), sem("mixg_done"), sem("var_done"), sem("rstd_done")
        h2_done, h2t_done, h2t_ev, logit_done = sem("h2_done"), sem("h2t_done"), sem("h2t_ev"), sem("logit_done")
        gsub_done, gexp_done, esub_done, eexp_done = sem("gsub_done"), sem("gexp_done"), sem("esub_done"), sem("eexp_done")
        mb_done, pos_done, hot_done, tab_done, slots_ready = (
            sem("mb_done"), sem("pos_done"), sem("hot_done"), sem("tab_done"), sem("slots_ready"))
        flag_ready = sem("flag_ready")
        shift_done, normed = sem("shift_done"), sem("normed")
        x1_done, pool_did, dve_did = sem("x1_done"), sem("pool_did"), sem("dve_did")
        xe_done, xe_ev, gu_done, silu_done, hid_done = (
            sem("xe_done"), sem("xe_ev"), sem("gu_done"), sem("silu_done"), sem("hid_done"))
        tr_done, tr_ev, dn_done, y_ev = sem("tr_done"), sem("tr_ev"), sem("dn_done"), sem("y_ev")
        centred, divided, fin_done = sem("centred"), sem("divided"), [sem(f"fin_done{i}") for i in range(TC)]

        def wait(eng, s, n):
            if not isinstance(n, int) or n > 0:
                eng.wait_ge(s, n)

        def w_cols(i):
            return slice(i * CW, (i + 1) * CW)

        def acc_of(i):
            return acc_cols[:, w_cols(i)] if i < ADA1 else acc_rows[:, w_cols(i - ADA1)]

        def conv_before(kind, f):
            return CONV_OUT.index((kind, f)) + 1

        PROJ_USED = [2, 4, 6, 8, 12, 16]
        w_at = {("w", w): n for n, w in enumerate(W_ORDER)}
        stage_at = {what: n for n, what in enumerate(SEQ)}

        def landed(eng, what):
            n = stage_at[what]
            eng.wait_ge(ld_stage[n % NSTG], 16 * (n // NSTG + 1))
            return stage[n % NSTG]

        def released(eng, what):
            if what[0] == "ada" and ADA_PE <= what[1] < ADA1:
                eng.wait_ge(ada_pe_done, what[1] - ADA_PE + 1)
            elif what[0] == "ada":
                eng.wait_ge(ada_done, what[1] + 1 - (ADA1 - ADA_PE if what[1] >= ADA1 else 0))
            elif w_at[what] < 6:
                eng.wait_ge(proj_done, PROJ_USED[w_at[what]])
            else:
                eng.wait_ge(conv_done, 2 * (w_at[what] - 5))

        def zbank(h):
            return flat[:, (h % 2) * 1536:(h % 2) * 1536 + ZW]

        def expert_weights(which, ex):
            w = which[0, bass.ds(ex, 1)]
            return w

        block = ctx.enter_context(nc.Block())

        @block.sync
        def _(sp):
            for n, (kind, i) in enumerate(SEQ):
                if n >= NSTG:
                    released(sp, SEQ[n - NSTG])
                src = w_ada[0].rearrange("(p k) n -> p k n", k=KC) if kind == "ada" else \
                    w_in[0].rearrange("(k p) n -> p k n", p=P)
                sp.dma_start(stage[n % NSTG][:], src[:, :, w_cols(i)]).then_inc(ld_stage[n % NSTG], 16)
            sp.dma_start(wo[:], w_out[0].rearrange("(k p) n -> p k n", p=P)).then_inc(ld_wo, 16)

            def load_gu(u, e, ex):
                for g, w in enumerate((w_gate, w_up)):
                    src = w[0, bass.ds(ex, 1)].rearrange("o (p k) f -> p (o k) f", k=KC)
                    sp.dma_start(w_gu[u][e][:, g], src).then_inc(ld_gu[u][e], 16)

            def load_dn(u, e, ex):
                src = w_down[0, bass.ds(ex, 1)].rearrange("o (a p) n -> p (o a) n", p=P)
                sp.dma_start(w_dn[u][e][:], src).then_inc(ld_dn[u][e], 16)

            sp.wait_ge(row_done, 8)
            for j in range(RING):
                if j == 1:
                    sp.wait_ge(av_done, NH // 2)
                    sp.wait_ge(conv_ev, len(CONV_OUT))
                if j == 2:
                    sp.wait_ge(out_done, 2 * TC)
                for e in range(2):
                    if (j, e) == (2, 1):
                        sp.wait_ge(logit_done, TC)
                        for n in range(2):
                            sp.wait_ge(st_h2[n], 32)
                    load_gu(j, e, j + e * HALF)
                    load_dn(j, e, j + e * HALF)

            def refill(i, u, first=False):
                j3 = RING * i - RING + u
                sp.wait_ge(gu_done, 2 * j3 + 1)
                load_gu(u, 0, RING * i + u)
                if not first:
                    sp.wait_ge(dn_done, 2 * j3)
                    load_dn((u - 1) % RING, 1, RING * i + u - 1 + HALF)
                sp.wait_ge(gu_done, 2 * j3 + 2)
                load_gu(u, 1, RING * i + u + HALF)
                sp.wait_ge(dn_done, 2 * j3 + 1)
                load_dn(u, 0, RING * i + u)

            for u in range(RING):
                refill(1, u, first=u == 0)
            with sp.Fori(2, NPAIR // RING) as i:
                for u in range(RING):
                    refill(i, u)
            refill(NPAIR // RING, 0)
            sp.wait_ge(dn_done, NE - 2 * RING)
            load_dn(0, 1, NPAIR - 1 + HALF)

            sp.wait_ge(flag_ready, 1)
            more = sp.value_load(flag[0:1, 0:1], min_val=0, max_val=NOVB)
            with sp.If(more > 0):
                with sp.Fori(0, NOVP) as j:
                    sp.wait_ge(dn_done, NE + 2 * j)
                    for e in range(2):
                        ex = sp.value_load(blk_exp[0:1, bass.ds(j + e * NOVP, 1)], min_val=0, max_val=NE - 1)
                        for g, w in enumerate((w_gate, w_up)):
                            sp.dma_start(w_gu[0][e][:, g], w[0, bass.ds(ex, 1)].rearrange("o (p k) f -> p (o k) f", k=KC)
                                         ).then_inc(ov_ld, 16)
                        sp.dma_start(w_dn[0][e][:], w_down[0, bass.ds(ex, 1)].rearrange("o (a p) n -> p (o a) n", p=P)
                                     ).then_inc(ov_ld, 16)
                sp.wait_ge(scattered[0], 16 * (LAST0 + NOVP))

            sp.wait_ge(dn_done, NE - 3)
            sp.dma_start(g2r[:], ln2_g[0].partition_broadcast(P)).then_inc(ld_g2, 16)
            sp.dma_start(bb2r[:], ln2_b[0].partition_broadcast(P)).then_inc(ld_g2, 16)
            for u in range(RING):
                sp.wait_ge(scattered[u], 16 * (NPAIR // RING + (u == 0)))
            for i in range(TC):
                for k in range(2):
                    sp.dma_start(y_tok[i][:, k], y_dram.rearrange("(i p k) n -> i k p n", p=P, k=2)[i, k]
                                 ).then_inc(ld_y[i][k], 16)
            for i in (0, 1, 3, 2):
                sp.wait_ge(fin_done[i], 1)
                sp.dma_start(out[0].rearrange("(i p) n -> i p n", p=P)[i], xs[:, i]).then_inc(st_out, 16)
            sp.wait_ge(st_out, 16 * TC)

        @block.gpsimd
        def _(pool):
            g = nc.gpsimd
            g.memset(b24[:], 0.0).then_inc(fills, 1)
            g.memset(ident[:], 0.0).then_inc(fills, 1)
            g.memset(ones[:], 1.0).then_inc(fills, 1)
            g.memset(ones_b[:], 1.0).then_inc(fills, 1)
            g.memset(neg_ones[:], -1.0).then_inc(fills, 1)
            g.memset(mh[:], -0.5).then_inc(fills, 1)
            g.iota(iota[:], [[1, P]], base=0, channel_multiplier=0, allow_small_or_imprecise_dtypes=True)
            g.iota(lowv[:], [[1, 2], [0, TC]], base=0, channel_multiplier=2, allow_small_or_imprecise_dtypes=True)
            g.iota(highv[:], [[0, 2], [2 * P, TC]], base=0, channel_multiplier=0, allow_small_or_imprecise_dtypes=True)
            pool.wait_ge(fills, 6)
            g.affine_select(out=ident[:], in_=ident[:], compare_op=ALU.not_equal, fill=1.0, base=0,
                            pattern=[[-1, P]], channel_multiplier=1).then_inc(consts, 1)
            g.affine_select(out=tri_neg[:], in_=neg_ones[:], compare_op=ALU.is_ge, fill=0.0, base=0,
                            pattern=[[-1, P]], channel_multiplier=1)
            g.affine_select(out=before[:], in_=ones_b[:], compare_op=ALU.is_gt, fill=0.0, base=0,
                            pattern=[[1, P]], channel_multiplier=-1)
            g.memset(qz[:], 0.0).then_inc(consts, 1)

            def mask(t):
                d = t[:, DIAG:DIAG + T].rearrange("p (j t) -> p j t", t=P)
                return g.affine_select(out=d, in_=d, compare_op=ALU.is_gt, fill=0.0, base=0,
                                       pattern=[[0, TC], [1, P]], channel_multiplier=-1)

            def mask_probs(h):
                pool.wait_ge(prob_done, h + 1)
                mask(expo[h % 4]).then_inc(prob_masked, 1)

            for h in range(NH):
                pool.wait_ge(sp_done, h + 1)
                mask(softp[h % 2]).then_inc(sp_masked, 1)
                if h > 0:
                    mask_probs(h - 1)
            mask_probs(NH - 1)

            pool.wait_ge(rows_ready, 1)
            g.tensor_scalar(g1r[:], g1r[:], ALPHA, None, ALU.mult).then_inc(scaled, 1)
            g.tensor_scalar(b1r[:], b1r[:], ALPHA, None, ALU.mult).then_inc(scaled, 1)

            def inv_std(n):
                pool.wait_ge(var_done, n + 1)
                g.tensor_tensor(rstd[:, n:n + 1], var_e[:, n:n + 1], mh[:], ALU.pow).then_inc(rstd_done, 1)

            def x1_rows(i):
                pool.wait_ge(scaled, 2)
                pool.wait_ge(normed, i + 1)
                g.tensor_tensor(xs[:, i], xs[:, i], g1r[:], ALU.mult).then_inc(pool_did, 1)
                pool.wait_ge(pool_did, i + 1)
                g.tensor_tensor(xs[:, i], xs[:, i], b1r[:], ALU.add).then_inc(x1_done, 1)

            def gather(j, buf, sem_done):
                g.indirect_dma_start(out=buf[:], out_offset=None, in_=h2_dram,
                                     in_offset=bass.IndirectOffsetOnAxis(ap=slot_tok[:, j:j + 1], axis=0),
                                     bounds_check=T - 1, oob_is_err=False).then_inc(sem_done, 16)

            def scatter(j, buf, sem_done):
                g.indirect_dma_start(out=y_dram, out_offset=bass.IndirectOffsetOnAxis(ap=slot_row[:, j:j + 1], axis=0),
                                     in_=buf[:], in_offset=None,
                                     bounds_check=2 * T - 1, oob_is_err=False).then_inc(sem_done, 16)

            def inv_std_shift(n):
                inv_std(n)
                pool.wait_ge(rstd_done, n + 1)
                g.tensor_tensor(shift_n[:, n:n + 1], neg_mean[:, n:n + 1], rstd[:, n:n + 1], ALU.mult).then_inc(shift_done, 1)

            for i in range(TC):
                inv_std_shift(i)
                if i > 0:
                    x1_rows(i - 1)
            pool.wait_ge(out_done, 2 * TC)
            g.memset(xg[0][:], 0.0).then_inc(xg_clear, 1)
            x1_rows(TC - 1)
            pool.wait_ge(x1_done, TC)
            g.memset(xg[1][:], 0.0).then_inc(xg_clear, 1)
            g.memset(xg[2][:], 0.0).then_inc(xg_clear, 1)
            pool.wait_ge(slots_ready, 1)
            for n in range(2):
                pool.wait_ge(st_h2[n], 32)
            for j in range(RING):
                pool.wait_ge(xg_clear, j + 1)
                gather(j, xg[j], gathered[j])
            for j in range(NPAIR):
                u = j % RING
                if j + RING < NPAIR:
                    pool.wait_ge(xe_done, j + 1)
                    gather(j + RING, xg[u], gathered[u])
                pool.wait_ge(y_ev, 2 * j + 2)
                scatter(j, ysb[u], scattered[u])

            pool.wait_ge(flag_ready, 1)
            more = pool.value_load(flag[0:1, 0:1], min_val=0, max_val=NOVB)
            with pool.If(more > 0):
                pool.wait_ge(xe_done, NPAIR)
                for j in range(NOVP):
                    pool.wait_ge(xe_done, NPAIR + j)
                    gather(NPAIR + j, xg[0], ov_gathered)
                    pool.wait_ge(y_ev, NE + 2 * j + 2)
                    scatter(NPAIR + j, ysb[0], scattered[0])
            def scale_shift(i):
                pool.wait_ge(divided, i + 1)
                if i < 2:
                    g.tensor_tensor(xs[:, i], xs[:, i], g2r[:], ALU.mult).then_inc(pool_did, 1)
                    pool.wait_ge(pool_did, TC + i + 1)
                g.tensor_tensor(xs[:, i], xs[:, i], bb2r[:], ALU.add).then_inc(fin_done[i], 1)

            inv_std_shift(TC)
            inv_std_shift(TC + 1)
            scale_shift(0)
            inv_std(TC + 2)
            scale_shift(1)
            inv_std(TC + 3)
            scale_shift(2)

        @block.scalar
        def _(act):
            s = nc.scalar
            s.preload_act_table_set("natural_log_exp_and_others")
            act.dma_start(csil[:, 0], c[0].rearrange("(p k) -> p k", k=KC)).then_inc(ld_c, 16)
            act.dma_start(conv_rows[0:CONV_W * NF, :], conv_w[0].rearrange("w (f p) -> (w f) p", p=P)).then_inc(ld_cw, 16)
            act.wait_ge(fills, 1)
            act.dma_start(b24[0:NADACH, :], b_ada[0].rearrange("(i n) -> i n", n=CW)).then_inc(ld_b24, 16)
            act.dma_start(xs[:], x[0].rearrange("(i p) n -> p i n", p=P)).then_inc(ld_x, 16)
            act.wait_ge(ld_c, 16)
            s.activation(csil[:, 1], csil[:, 0], ACT.Exp, scale=-1.0).then_inc(exp_c, 1)
            act.dma_start(w_r[:, :, 0:NG], w_router_group[0].rearrange("(p k) g -> p k g", k=KC)).then_inc(ld_wr, 16)
            act.dma_start(w_r[:, :, NG:], w_router_expert[0].rearrange("(p k) g -> p k g", k=KC)).then_inc(ld_wr, 16)
            act.dma_start(b_r[:, 0:NG], b_router_group[0].partition_broadcast(P)).then_inc(ld_br, 16)
            act.dma_start(b_r[:, NG:], b_router_expert[0].partition_broadcast(P)).then_inc(ld_br, 16)
            for k in range(KC):
                act.wait_ge(xt_done, k + 1)
                s.copy(hT[:, k], ps[:, k % 4, :]).then_inc(xt_ev, 1)

            act.wait_ge(consts, 2)
            for n in range(16):
                act.wait_ge(proj_done, n + 1)
                src = ps[:, n % 4]
                if n < 4:
                    s.mul(qz[0:HD, 2 * n], src[0:HD], HD ** -0.5)
                    s.mul(qz[HD:P, 2 * n + 1], src[HD:P], HD ** -0.5).then_inc(proj_ev, 1)
                elif n < 8:
                    s.copy(kT[:, n - 4], src).then_inc(proj_ev, 1)
                else:
                    half, i = divmod(n - 8, TC)
                    s.copy(v[:, i, w_cols(half)], src[:, 0:CW]).then_inc(proj_ev, 1)

            def softplus_tail(h):
                e = expo[h % 4]
                act.wait_ge(z_done, h + 1)
                if h >= 4:
                    act.wait_ge(av_done, (h - 4) // 2 + 1)
                s.activation(e[:], zbank(h), ACT.Abs).then_inc(abs_done, 1)
                act.wait_ge(abs_done, h + 1)
                s.activation(e[:], e[:], ACT.Exp, scale=-1.0).then_inc(exp_done, 1)
                act.wait_ge(exp_done, h + 1)
                s.activation(e[:], e[:], ACT.Ln, bias=1.0).then_inc(ln_done, 1)

            def av_out(p):
                act.wait_ge(av_done, p + 1)
                s.copy(mixT[:, p], ps[:, 7]).then_inc(av_ev, 1)

            softplus_tail(0)
            for h in range(NH):
                for n in range(CONV_AT[h], CONV_AT[h + 1]):
                    kind, f = CONV_OUT[n]
                    if kind == "cc":
                        act.wait_ge(conv_done, n + 1)
                        if f >= 2:
                            act.wait_ge(conv_ev, conv_before("cb", f - 2))
                        s.copy(cc_sb[f % 2][:], ps[:, 6]).then_inc(conv_ev, 1)
                if h + 1 < NH:
                    softplus_tail(h + 1)
                if h > 0 and h % 2 == 0:
                    av_out(h // 2 - 1)
                act.wait_ge(tri_done, h + 1)
                act.wait_ge(sp_done, h + 1)
                s.activation(expo[h % 4][:], zbank(h), ACT.Exp).then_inc(prob_done, 1)
            av_out(NH // 2 - 1)
            act.dma_start(g1r[:], ln1_g[0].partition_broadcast(P)).then_inc(ld_g1, 16)
            act.dma_start(b1r[:], ln1_b[0].partition_broadcast(P)).then_inc(ld_b1, 16)

            act.wait_ge(conv_done, len(CONV_OUT))
            for r in range(8):
                act.wait_ge(row_done, r + 1)
                dst = (gate1r, b2r, a2r, gate2r)[r // 2]
                s.copy(dst[:, (r % 2) * 512:(r % 2 + 1) * 512], ps[:, r % 4]).then_inc(row_ev, 1)
            for i in range(TC):
                act.wait_ge(h2_done, i + 1)
                act.dma_start(h2_dram.rearrange("(i p) n -> i p n", p=P)[i], h2p[i % 2][:]).then_inc(st_h2[i % 2], 16)
                act.wait_ge(h2t_done, i + 1)
                if i > 0:
                    act.wait_ge(logit_done, i)
                s.copy(h2T.rearrange("p k t -> p (k t)"), flat[:, 0:D]).then_inc(h2t_ev, 1)
                act.wait_ge(shift_done, i + 1)
                s.activation(xs[:, i], xs[:, i], ACT.Identity, scale=rstd[:, i:i + 1], bias=shift_n[:, i:i + 1]
                             ).then_inc(normed, 1)

            act.wait_ge(gsub_done, 1)
            s.activation(g4[:, 1], g4[:, 0], ACT.Exp).then_inc(gexp_done, 1)
            act.wait_ge(esub_done, 1)
            s.activation(sc[:, 2, 0], sc[:, 1, 0], ACT.Exp).then_inc(eexp_done, 1)

            def xe_copy(j, u):
                act.wait_ge(xe_done, j + 1)
                if not isinstance(j, int) or j >= RING:
                    act.wait_ge(gu_done, 2 * j - 2 * RING + 2)
                s.copy(xT[u].rearrange("p k t -> p (k t)"), flat[:, 0:D]).then_inc(xe_ev, 1)

            def hid_t(y, e):
                act.wait_ge(tr_done, y + 1)
                if not isinstance(y, int) or y >= 2:
                    act.wait_ge(dn_done, y - 1)
                s.copy(hidT[e][:], ps[:, 4 + e, 0:P]).then_inc(tr_ev, 1)

            def silu(y, e):
                act.wait_ge(gu_done, y + 1)
                if not isinstance(y, int) or y >= 2:
                    act.wait_ge(hid_done, y - 1)
                s.activation(silu_sb[e][:], ps[:, 2 + e, 0:P], ACT.Silu).then_inc(silu_done, 1)

            def pair(i, u, first=False, last=False):
                j = RING * i + u
                if not first:
                    hid_t(2 * j - 1, 1)
                silu(2 * j, 0)
                hid_t(2 * j, 0)
                silu(2 * j + 1, 1)
                if not last:
                    xe_copy(j + 1, (u + 1) % RING)

            xe_copy(0, 0)
            for u in range(RING):
                pair(0, u, first=u == 0)
            with act.Fori(1, NPAIR // RING) as i:
                for u in range(RING):
                    pair(i, u)
            pair(NPAIR // RING, 0, last=True)
            hid_t(NE - 1, 1)

            act.wait_ge(flag_ready, 1)
            more = act.value_load(flag[0:1, 0:1], min_val=0, max_val=NOVB)
            with act.If(more > 0):
                with act.Fori(0, NOVP) as j:
                    act.wait_ge(xe_done, NPAIR + j + 1)
                    s.copy(xT[0].rearrange("p k t -> p (k t)"), flat[:, 0:D]).then_inc(xe_ev, 1)
                    for e in range(2):
                        act.wait_ge(gu_done, NE + 2 * j + e + 1)
                        s.activation(silu_sb[e][:], ps[:, 2 + e, 0:P], ACT.Silu).then_inc(silu_done, 1)
                        act.wait_ge(tr_done, NE + 2 * j + e + 1)
                        s.copy(hidT[e][:], ps[:, 4 + e, 0:P]).then_inc(tr_ev, 1)
            for i in range(TC - 1):
                act.wait_ge(rstd_done, TC + i + 1)
                if i < 2:
                    act.wait_ge(shift_done, TC + i + 1)
                    s.activation(xs[:, i], xs[:, i], ACT.Identity, scale=rstd[:, TC + i:TC + i + 1],
                                 bias=shift_n[:, TC + i:TC + i + 1]).then_inc(divided, 1)
                    continue
                act.wait_ge(centred, 1)
                s.mul(xs[:, i], xs[:, i], rstd[:, TC + i:TC + i + 1]).then_inc(divided, 1)

        @block.vector
        def _(dve):
            w = nc.vector
            count = [0]

            def did(ins):
                count[0] += 1
                ins.then_inc(dve_did, 1)

            def settle():
                dve.wait_ge(dve_did, count[0])

            def link(ins):
                did(ins)
                settle()

            dve.wait_ge(exp_c, 1)
            link(w.tensor_scalar(csil[:, 2], csil[:, 1], 1.0, None, ALU.add))
            link(w.reciprocal(csil[:, 1], csil[:, 2]))
            w.tensor_tensor(csil[:, 3], csil[:, 0], csil[:, 1], ALU.mult).then_inc(cs_ready, 1)
            dve.wait_ge(cs_ready, 1)

            def ada(i):
                st = landed(dve, ("ada", i))
                acc = acc_of(i)
                link(w.tensor_scalar(acc, st[:, 0], csil[:, 3, 0:1], None, ALU.mult))
                for k in range(1, KC):
                    link(w.scalar_tensor_tensor(out=acc, in0=st[:, k], scalar=csil[:, 3, k:k + 1], in1=acc,
                                                op0=ALU.mult, op1=ALU.add))
                w.scalar_tensor_tensor(out=acc, in0=b24[:], scalar=ident[:, i:i + 1], in1=acc,
                                       op0=ALU.mult, op1=ALU.add).then_inc(ada_done, 1)

            dve.wait_ge(ld_b24, 16)
            dve.wait_ge(consts, 1)
            for i in range(ADA_PE):
                ada(i)
            dve.wait_ge(cw_done, 1)
            w.tensor_copy(cwT[:], ps[:, 6, 0:CONV_W * NF]).then_inc(cw_ev, 1)
            dve.wait_ge(cols_done, 1)
            link(w.tensor_copy(colsb[:, 0:KC], ps[:, 7, 0:KC]))
            link(w.tensor_scalar(colsb[:, KC:], ps[:, 7, KC:2 * KC], 1.0, None, ALU.add))
            for k in range(KC):
                dve.wait_ge(xt_ev, k + 1)
                w.tensor_scalar(hT[:, k], hT[:, k], colsb[:, KC + k:KC + k + 1], colsb[:, k:k + 1],
                                ALU.mult, ALU.add).then_inc(ht_done, 1)
            for i in range(ADA1, 20):
                ada(i)

            def softplus(h):
                dve.wait_ge(ln_done, h + 1)
                if h >= 2:
                    dve.wait_ge(tri_done, h - 1)
                w.scalar_tensor_tensor(out=softp[h % 2][:], in0=zbank(h), scalar=0.0, in1=expo[h % 4][:],
                                       op0=ALU.max, op1=ALU.add).then_inc(sp_done, 1)

            def suffix_sums(h):
                f, sx = softp[h % 2], suffix[h % 2]
                dve.wait_ge(sp_masked, h + 1)
                did(w.tensor_tensor(sx[:, 0:P], f[:, DIAG + 3 * P:DIAG + 4 * P], f[:, OFF2:OFF2 + P], ALU.add))
                did(w.tensor_tensor(sx[:, P:2 * P], f[:, DIAG + 2 * P:DIAG + 3 * P], f[:, OFF1:OFF1 + P], ALU.add))
                settle()
                w.tensor_tensor(sx[:, 2 * P:3 * P], f[:, OFF1 + P:OFF1 + 2 * P], sx[:, 0:P], ALU.add).then_inc(suf_done, 1)

            def conv(n):
                kind, f = CONV_OUT[n]
                y, u = cc_sb[f % 2], u_conv
                if kind == "cc":
                    return
                dve.wait_ge(conv_done, n + 1)
                dve.wait_ge(conv_ev, n)
                settle()
                if kind == "cx":
                    w.tensor_tensor(u[:], ps[:, 6], y[:], ALU.mult).then_inc(conv_ev, 1)
                    dve.wait_ge(conv_ev, n + 1)
                    link(w.tensor_scalar(y[:], u[:], cwT[:, 2 * NF + f:2 * NF + f + 1], None, ALU.mult))
                    link(w.scalar_tensor_tensor(out=y[:, 1:], in0=u[:, :T - 1], scalar=cwT[:, NF + f:NF + f + 1],
                                                in1=y[:, 1:], op0=ALU.mult, op1=ALU.add))
                    did(w.scalar_tensor_tensor(out=y[:, 2:], in0=u[:, :T - 2], scalar=cwT[:, f:f + 1],
                                               in1=y[:, 2:], op0=ALU.mult, op1=ALU.add))
                else:
                    w.tensor_tensor(mixT[:, NF + f], ps[:, 6], y[:], ALU.mult).then_inc(conv_ev, 1)

            dve.wait_ge(cw_ev, 1)
            for h in range(NH):
                softplus(h)
                suffix_sums(h)
                for n in range(CONV_AT[h], CONV_AT[h + 1]):
                    conv(n)
                if 20 + h < NADACH:
                    ada(20 + h)

            dve.wait_ge(row_ev, 6)
            dve.wait_ge(ld_g1, 16)
            dve.wait_ge(ld_b1, 16)
            dve.wait_ge(tri_done, NH)
            link(w.tensor_scalar(a2r[:], a2r[:], 1.0, None, ALU.add))
            link(w.tensor_tensor(h2nat[:], a2r[:], b1r[:], ALU.mult))
            did(w.tensor_tensor(b2r[:], b2r[:], h2nat[:], ALU.add))
            link(w.tensor_tensor(a2r[:], a2r[:], g1r[:], ALU.mult))
            w.engine_nop().then_inc(rows_ready, 1)

            def moments(n):
                settle()
                link(w.bn_aggr(mv[:, n], bn[:]))
                if n < TC + 2:
                    did(w.tensor_scalar(neg_mean[:, n:n + 1], mv[:, n, 0:1], -1.0, None, ALU.mult))
                w.tensor_scalar(var_e[:, n:n + 1], mv[:, n, 1:2], EPS, None, ALU.add).then_inc(var_done, 1)

            for i in range(TC):
                wait(dve, h2_done, i)
                for n in range(2):
                    cols = slice(n * 512, (n + 1) * 512)
                    dve.wait_ge(out_done, 2 * i + n + 1)
                    w.tensor_tensor(h2nat[:, cols], ps[:, 4 + 2 * (i % 2) + n], gate1r[:, cols], ALU.mult
                                    ).then_inc(mixg_done, 1)
                    dve.wait_ge(mixg_done, 2 * i + n + 1)
                    link(w.scalar_tensor_tensor(out=xs[:, i, cols], in0=xs[:, i, cols], scalar=ALPHA,
                                                in1=h2nat[:, cols], op0=ALU.mult, op1=ALU.add))
                    did(w.bn_stats(bn[:, n], xs[:, i, cols]))
                moments(i)
                did(w.scalar_tensor_tensor(out=h2nat[:], in0=xs[:, i], scalar=mv[:, i, 0:1], in1=a2r[:],
                                           op0=ALU.subtract, op1=ALU.mult))
                if i >= 2:
                    dve.wait_ge(st_h2[i % 2], 16)
                    dve.wait_ge(h2t_done, i - 1)
                dve.wait_ge(rstd_done, i + 1)
                settle()
                w.scalar_tensor_tensor(out=h2p[i % 2].rearrange("t (k p) -> t p k", k=KC),
                                       in0=h2nat.rearrange("t (p k) -> t p k", k=KC), scalar=rstd[:, i:i + 1],
                                       in1=b2r.rearrange("t (p k) -> t p k", k=KC),
                                       op0=ALU.mult, op1=ALU.add).then_inc(h2_done, 1)

            dve.wait_ge(h2_done, TC)
            dve.wait_ge(logit_done, TC)
            dve.wait_ge(ld_br, 32)
            link(w.tensor_tensor(lg[:], ps[:, 2, 0:TC * (NG + NE)].rearrange("p (c e) -> p c e", c=TC),
                                 b_r[:].unsqueeze(1).to_broadcast([P, TC, NG + NE]), ALU.add))

            def argmax(vals, best, eq, index, hot, n):
                bc = lambda t: t.unsqueeze(2).to_broadcast([P, TC, n])
                link(w.tensor_reduce(best, vals, AX, ALU.max))
                link(w.tensor_tensor(eq, vals, bc(best), ALU.is_equal))
                link(w.scalar_tensor_tensor(out=eq, in0=eq, scalar=-64.0,
                                            in1=iota[:, 0:n].unsqueeze(1).to_broadcast([P, TC, n]),
                                            op0=ALU.mult, op1=ALU.add))
                link(w.tensor_reduce(index, eq, AX, ALU.min))
                link(w.tensor_tensor(hot, eq, bc(index), ALU.is_equal))

            gmax, gidx, gsum, gprob = sc[:, 0, 0], sc[:, 0, 1], sc[:, 2, 1], sc[:, 1, 1]
            m1, m2 = sc[:, 3, 0], sc[:, 3, 1]
            ei = sc[:, 4]
            ghot = g4[:, 2]
            lgg = lg[:, :, 0:NG]
            argmax(lgg, gmax, ghot, gidx, ghot, NG)
            w.tensor_tensor(g4[:, 0], lgg, gmax.unsqueeze(2).to_broadcast([P, TC, NG]), ALU.subtract).then_inc(gsub_done, 1)
            link(w.tensor_scalar(ghot, ghot, 1.0, BIG, ALU.subtract, ALU.mult))
            link(w.tensor_tensor(lem.rearrange("p c (g e) -> p c g e", g=NG),
                                 lg[:, :, NG:].rearrange("p c (g e) -> p c g e", g=NG),
                                 ghot.unsqueeze(3).to_broadcast([P, TC, NG, EPG]), ALU.add))
            argmax(lem[:], m1, t32[:], ei[:, 0], oh[:, 0], NE)
            link(w.scalar_tensor_tensor(out=lem[:], in0=oh[:, 0], scalar=-3 * BIG, in1=lem[:], op0=ALU.mult, op1=ALU.add))
            argmax(lem[:], m2, t32[:], ei[:, 1], oh[:, 1], NE)
            w.tensor_tensor(sc[:, 1, 0], m2, m1, ALU.subtract).then_inc(esub_done, 1)
            w.tensor_tensor(mb[:], oh[:, 0], oh[:, 1], ALU.add).then_inc(mb_done, 1)

            kc8 = lambda t: t.rearrange("p k c -> p (k c)")
            ot = oh_t.rearrange("p k c e -> p (k c e)")
            MO = T // SLOTS - 1

            def pick(dst, per_expert):
                link(w.tensor_tensor(oh_t[:], oh[:], per_expert, ALU.mult))
                link(w.tensor_reduce(dst, oh_t[:], AX, ALU.add))

            def column_hot(hot, col, n):
                colb = kc8(col).unsqueeze(2).to_broadcast([P, 8, n])
                link(w.tensor_tensor(hot[:, :, 2], colb, iota[:, 0:n].unsqueeze(1).to_broadcast([P, 8, n]), ALU.is_equal))
                for part, vals in enumerate((lowv, highv)):
                    did(w.tensor_tensor(hot[:, :, part], hot[:, :, 2], kc8(vals[:]).unsqueeze(2).to_broadcast([P, 8, n]),
                                        ALU.mult))

            def row_hot(row):
                return w.tensor_tensor(rowhot[:], kc8(row).unsqueeze(2).to_broadcast([P, 8, P]),
                                       iota[:].unsqueeze(1).to_broadcast([P, 8, P]), ALU.is_equal)

            def slots_of(tab, first, n):
                ta, tb = lem.rearrange("p c e -> p (c e)")[:, 0:n], lem.rearrange("p c e -> p (c e)")[:, n:2 * n]
                link(w.tensor_scalar(ta, tab[:, 2], -1.0, -float(SKIP), ALU.add, ALU.mult))
                link(w.tensor_tensor(tb, tab[:, 0], ta, ALU.add))
                link(w.tensor_tensor(slot_row[:, first:first + n], tab[:, 1], tb, ALU.add))
                return w.tensor_scalar(slot_tok[:, first:first + n], slot_row[:, first:first + n], 1, None,
                                       ALU.logical_shift_right)

            pos, blk0, over, q, colv, rowv, beyond, q2, colo, tmp = (sc[:, n] for n in range(5, 15))
            link(w.tensor_scalar(ei, ei, 64.0, None, ALU.add))
            link(w.tensor_scalar(q, ei, float(HALF), None, ALU.is_ge))
            link(w.scalar_tensor_tensor(out=colv, in0=q, scalar=-float(HALF), in1=ei, op0=ALU.mult, op1=ALU.add))
            column_hot(colhot, colv, NPAIR)
            dve.wait_ge(pos_done, 1)
            pick(pos, ps[:, 5, 0:TC * NE].rearrange("p (c e) -> p c e", c=TC).unsqueeze(1).to_broadcast([P, 2, TC, NE]))
            link(w.tensor_scalar(beyond, pos, float(SLOTS), None, ALU.is_ge))
            link(w.scalar_tensor_tensor(out=rowv, in0=q, scalar=float(SLOTS), in1=pos, op0=ALU.mult, op1=ALU.add))
            link(w.scalar_tensor_tensor(out=rowv, in0=beyond, scalar=float(NOWHERE), in1=rowv, op0=ALU.mult, op1=ALU.add))
            row_hot(rowv).then_inc(hot_done, 1)
            dve.wait_ge(tab_done, 1)
            slots_of(ps[:, 4, 0:3 * NPAIR].rearrange("p (s n) -> p s n", s=3), 0, NPAIR).then_inc(slots_ready, 1)

            dve.wait_ge(gexp_done, 1)
            link(w.tensor_reduce(gsum, g4[:, 1], AX, ALU.add))
            dve.wait_ge(eexp_done, 1)
            link(w.scalar_tensor_tensor(out=gprob, in0=sc[:, 2, 0], scalar=1.0, in1=gsum, op0=ALU.add, op1=ALU.mult))
            link(w.reciprocal(wk[:, 0], gprob))
            link(w.tensor_tensor(wk[:, 1], wk[:, 0], sc[:, 2, 0], ALU.mult))

            def blocks_beyond(dst, count, n, least):
                over_m = ot[:, 0:n * MO].rearrange("p (e m) -> p e m", m=MO)
                link(w.tensor_tensor(over_m, count.unsqueeze(2).to_broadcast([P, n, MO]),
                                     iota[:, 1:MO + 1].unsqueeze(1).to_broadcast([P, n, MO]), least))
                link(w.tensor_reduce(dst, over_m, AX, ALU.add))

            C0 = cum[0][:, 16:]
            nov, blocks = t32[:, 0], t32[:, 2]
            did(w.memset(cum[0][:, 0:16], 0.0))
            did(w.memset(cum[1][:, 0:16], 0.0))
            link(w.tensor_scalar(blocks, ps[:, 5, P:P + NE], 1.0 / SLOTS, None, ALU.mult))
            blocks_beyond(nov, blocks, NE, ALU.is_gt)
            link(w.tensor_copy(C0, nov))
            src, dst = 0, 1
            for d in (1, 2, 4, 8, 16):
                link(w.tensor_tensor(cum[dst][:, 16:], cum[src][:, 16:], cum[src][:, 16 - d:16 - d + NE], ALU.add))
                src, dst = dst, src
            incl = cum[src][:, 16:]
            first_blk = t32[:, 1]
            link(w.tensor_tensor(first_blk, incl, nov, ALU.subtract))
            pick(blk0, first_blk.unsqueeze(1).unsqueeze(1).to_broadcast([P, 2, TC, NE]))
            link(w.tensor_scalar(tmp, pos, 1.0 / SLOTS, None, ALU.mult))
            blocks_beyond(kc8(over), kc8(tmp), 8, ALU.is_ge)
            link(w.scalar_tensor_tensor(out=colo, in0=blk0, scalar=-1.0, in1=over, op0=ALU.add, op1=ALU.add))
            link(w.tensor_scalar(q2, colo, float(NOVP), None, ALU.is_ge))
            link(w.scalar_tensor_tensor(out=colo, in0=q2, scalar=-float(NOVP), in1=colo, op0=ALU.mult, op1=ALU.add))
            link(w.tensor_tensor(tmp, q2, over, ALU.subtract))
            link(w.scalar_tensor_tensor(out=rowv, in0=tmp, scalar=float(SLOTS), in1=pos, op0=ALU.mult, op1=ALU.add))
            link(w.tensor_scalar(tmp, beyond, -1.0, -float(NOWHERE), ALU.add, ALU.mult))
            link(w.tensor_tensor(rowv, rowv, tmp, ALU.add))
            for half in range(2):
                b3 = oh_t[:].rearrange("p k c e -> p (k c) e")
                link(w.tensor_tensor(b3, incl.unsqueeze(1).to_broadcast([P, 8, NE]),
                                     iota[:, 8 * half:8 * half + 8].unsqueeze(2).to_broadcast([P, 8, NE]), ALU.is_le))
                link(w.tensor_reduce(sc[:, 15 + half].rearrange("p k c -> p (k c)"), b3, AX, ALU.add))
            link(w.tensor_scalar(blk_exp[:], sc[:, 15:17].rearrange("p n k c -> p (n k c)"), float(NE - 1), None, ALU.min))
            column_hot(colhot_ov, colo, NOVP)
            settle()
            row_hot(rowv).then_inc(hot_done, 1)

            def overflow_slots():
                dve.wait_ge(tab_done, 2)
                link(slots_of(ps[:, 5, OVT:OVT + 3 * NOVP].rearrange("p (s n) -> p s n", s=3), NPAIR, NOVP))
                w.tensor_copy(flag[:], incl[:, NE - 1:NE]).then_inc(flag_ready, 1)
                dve.wait_ge(flag_ready, 1)

            def hidden(y, e):
                dve.wait_ge(silu_done, y + 1)
                if not isinstance(y, int) or y >= 2:
                    dve.wait_ge(tr_done, y - 1)
                w.tensor_tensor(hid[e][:], ps[:, 2 + e, P:2 * P], silu_sb[e][:], ALU.mult).then_inc(hid_done, 1)

            def y_out(y, e, u, i=0):
                dve.wait_ge(dn_done, y + 1)
                if e == 0 and (not isinstance(i, int) or i > 0):
                    dve.wait_ge(scattered[u], 16 * i)
                for b in range(2):
                    ins = w.tensor_tensor(ysb[u][e * HD:(e + 1) * HD, b * 512:(b + 1) * 512],
                                          ps[b * HD:(b + 1) * HD, 6 + e, :],
                                          gate2r[b * HD:(b + 1) * HD, b * 512:(b + 1) * 512], ALU.mult)
                ins.then_inc(y_ev, 1)

            def pair(i, u, first=False):
                j = RING * i + u
                hidden(2 * j, 0)
                if first:
                    overflow_slots()
                else:
                    y_out(2 * j - 1, 1, (u - 1) % RING)
                hidden(2 * j + 1, 1)
                y_out(2 * j, 0, u, i)

            dve.wait_ge(row_ev, 8)
            for u in range(RING):
                pair(0, u, first=u == 0)
            with dve.Fori(1, NPAIR // RING) as i:
                for u in range(RING):
                    pair(i, u)
            pair(NPAIR // RING, 0)
            y_out(NE - 1, 1, 0)

            more = dve.value_load(flag[0:1, 0:1], min_val=0, max_val=NOVB)
            with dve.If(more > 0):
                with dve.Fori(0, NOVP) as j:
                    dve.wait_ge(scattered[0], 16 * LAST0 + 16 * j)
                    for e in range(2):
                        dve.wait_ge(silu_done, NE + 2 * j + e + 1)
                        w.tensor_tensor(hid[e][:], ps[:, 2 + e, P:2 * P], silu_sb[e][:], ALU.mult).then_inc(hid_done, 1)
                        dve.wait_ge(dn_done, NE + 2 * j + e + 1)
                        for b in range(2):
                            ins = w.tensor_tensor(ysb[0][e * HD:(e + 1) * HD, b * 512:(b + 1) * 512],
                                                  ps[b * HD:(b + 1) * HD, 6 + e, :],
                                                  gate2r[b * HD:(b + 1) * HD, b * 512:(b + 1) * 512], ALU.mult)
                        ins.then_inc(y_ev, 1)

            dve.wait_ge(ld_g2, 32)
            for i in range(TC):
                dve.wait_ge(x1_done, i + 1)
                for k in range(2):
                    dve.wait_ge(ld_y[i][k], 16)
                    link(w.scalar_tensor_tensor(out=xs[:, i], in0=y_tok[i][:, k], scalar=wk[:, k, i:i + 1],
                                                in1=xs[:, i], op0=ALU.mult, op1=ALU.add))
                for n in range(2):
                    did(w.bn_stats(bn[:, n], xs[:, i, n * 512:(n + 1) * 512]))
                moments(TC + i)
                if i < 2:
                    continue
                w.scalar_tensor_tensor(out=xs[:, i], in0=xs[:, i], scalar=mv[:, TC + i, 0:1], in1=g2r[:],
                                       op0=ALU.subtract, op1=ALU.mult).then_inc(centred, 1)
            i = TC - 1
            dve.wait_ge(centred, 2)
            dve.wait_ge(rstd_done, 2 * TC)
            w.scalar_tensor_tensor(out=xs[:, i], in0=xs[:, i], scalar=rstd[:, TC + i:TC + i + 1], in1=bb2r[:],
                                   op0=ALU.mult, op1=ALU.add).then_inc(fin_done[i], 1)

        @block.tensor
        def _(pe):
            t = nc.tensor
            pe.wait_ge(consts, 1)
            pe.wait_ge(ld_cw, 16)
            n_cw = CONV_W * NF
            t.transpose(ps[:, 6, 0:n_cw], conv_rows[0:n_cw, :], ident[0:n_cw, 0:n_cw]).then_inc(cw_done, 1)


            def ada_cols(i):
                st = landed(pe, ("ada", i))
                for f in range(CW // P):
                    col = ps[:, 7, i * (CW // P) + f:i * (CW // P) + f + 1]
                    for k in range(KC):
                        t.matmul(col, st[:, k, f * P:(f + 1) * P], csil[:, 3, k:k + 1], start=k == 0, stop=False)
                    ins = t.matmul(col, b24[:, f * P:(f + 1) * P], ident[:, i:i + 1], start=False, stop=True)
                ins.then_inc(ada_pe_done, 1)

            pe.wait_ge(cs_ready, 1)
            pe.wait_ge(ld_b24, 16)
            ada_cols(ADA_PE)
            pe.wait_ge(ld_x, 16)
            for k in range(KC):
                if k >= 4:
                    pe.wait_ge(xt_ev, k - 3)
                for i in range(TC):
                    ins = t.transpose(ps[:, k % 4, i * P:(i + 1) * P], xs[:, i, k * P:(k + 1) * P], ident[:])
                ins.then_inc(xt_done, 1)
                if k == 3:
                    ada_cols(ADA_PE + 1)
            for i in range(ADA_PE + 2, ADA1):
                ada_cols(i)
            for k in range(ADA_PE * CW // P):
                pe.wait_ge(ada_done, k * P // CW + 1)
                ins = t.matmul(ps[:, 7, k:k + 1], acc_cols[:, k * P:(k + 1) * P], ones[:, 0:1], start=True, stop=True)
            ins.then_inc(cols_done, 1)

            pe.wait_ge(xt_ev, KC)
            out_n = [0]

            def proj_bank():
                n = out_n[0]
                if n >= 4:
                    pe.wait_ge(proj_ev, n - 3)
                out_n[0] += 1
                return ps[:, n % 4]

            for wi in W_ORDER[:4]:
                st = landed(pe, ("w", wi))
                for f in range(CW // P):
                    dst = proj_bank()
                    for k in range(KC):
                        if out_n[0] == 1:
                            pe.wait_ge(ht_done, k + 1)
                        ins = t.matmul(dst, st[:, k, f * P:(f + 1) * P], hT[:, k], start=k == 0, stop=k == KC - 1)
                    ins.then_inc(proj_done, 1)
            for wi in W_ORDER[4:6]:
                st = landed(pe, ("w", wi))
                for i in range(TC):
                    dst = proj_bank()
                    for k in range(KC):
                        ins = t.matmul(dst[:, 0:CW], hT[:, k, i * P:(i + 1) * P], st[:, k], start=k == 0, stop=k == KC - 1)
                    ins.then_inc(proj_done, 1)

            def scores(h):
                z, f = zbank(h), h // 2
                if h >= 2:
                    pe.wait_ge(prob_done, h - 1)
                key = lambda j: kT[:, f, j * P:(j + 1) * P]
                for j in range(TC):
                    t.matmul(z[:, DIAG + j * P:DIAG + (j + 1) * P], key(j), qz[:, h, j * P:(j + 1) * P],
                             start=j == 0, stop=False, skip_group_check=True)
                t.matmul(z[:, OFF0:OFF0 + 3 * P], key(0), qz[:, h, P:T], start=True, stop=False, skip_group_check=True)
                t.matmul(z[:, OFF2:OFF2 + P], key(2), qz[:, h, 3 * P:T], start=False, stop=False, skip_group_check=True)
                t.matmul(z[:, OFF1:OFF1 + 2 * P], key(1), qz[:, h, 2 * P:T], start=True, stop=False,
                         skip_group_check=True).then_inc(z_done, 1)

            def conv_proj(n):
                kind, f = CONV_OUT[n]
                wi = {"cc": CC, "cx": CX, "cb": CB}[kind] + f // 2
                st = landed(pe, ("w", wi))
                if n > 0:
                    pe.wait_ge(conv_ev, n)
                for k in range(KC):
                    ins = t.matmul(ps[:, 6], st[:, k, (f % 2) * P:(f % 2 + 1) * P], hT[:, k], start=k == 0, stop=k == KC - 1)
                ins.then_inc(conv_done, 1)

            def attend(p):
                pe.wait_ge(prob_masked, 2 * p + 2)
                if p > 0:
                    pe.wait_ge(av_ev, p)
                parts = [(slice(j * P, (j + 1) * P), j, DIAG + j * P, P) for j in range(TC)]
                parts += [(slice(P, T), 0, OFF0, 3 * P), (slice(2 * P, T), 1, OFF1, 2 * P), (slice(3 * P, T), 2, OFF2, P)]
                for n, (cols, j, first, width) in enumerate(parts):
                    for h in (2 * p, 2 * p + 1):
                        b = (h % 2) * HD
                        ins = t.matmul(ps[b:b + HD, 7, cols], v[:, j, h * HD:(h + 1) * HD],
                                       expo[h % 4][:, first:first + width], start=n == 0,
                                       stop=n == len(parts) - 1, skip_group_check=True)
                ins.then_inc(av_done, 1)

            def later_keys(h):
                z, f, sx = zbank(h), softp[h % 2], suffix[h % 2]
                pe.wait_ge(suf_done, h + 1)
                add = lambda to, m, r, stop=False: t.matmul(to, m, r, start=False, stop=stop, skip_group_check=True)
                add(z[:, 0:512], tri_neg[:], f[:, 0:512], True)
                add(z[:, 512:1024], tri_neg[:], f[:, 512:1024])
                add(z[:, 1024:ZW], tri_neg[:], f[:, 1024:ZW])
                add(z[:, OFF0:OFF0 + P], neg_ones[:], f[:, DIAG + P:DIAG + 2 * P])
                add(z[:, OFF0 + P:OFF0 + 3 * P], neg_ones[:], sx[:, P:3 * P])
                add(z[:, OFF2:OFF2 + P], neg_ones[:], f[:, DIAG + 3 * P:DIAG + 4 * P], True)
                add(z[:, OFF1:OFF1 + P], neg_ones[:], f[:, DIAG + 2 * P:DIAG + 3 * P])
                add(z[:, OFF1 + P:OFF1 + 2 * P], neg_ones[:], sx[:, 0:P], True).then_inc(tri_done, 1)

            pe.wait_ge(proj_ev, 16)
            pe.wait_ge(cw_ev, 1)
            scores(0)
            for h in range(NH):
                if h + 1 < NH:
                    scores(h + 1)
                for n in range(CONV_AT[h], CONV_AT[h + 1]):
                    conv_proj(n)
                if h > 0 and h % 2 == 0:
                    attend(h // 2 - 1)
                later_keys(h)
            attend(NH // 2 - 1)

            pe.wait_ge(ada_done, NADACH - (ADA1 - ADA_PE))
            pe.wait_ge(prob_done, NH)
            for r in range(8):
                if r >= 4:
                    pe.wait_ge(row_ev, r - 3)
                t.matmul(ps[:, r % 4], ones[:], acc_rows[:, r * 512:(r + 1) * 512], start=True, stop=True).then_inc(row_done, 1)

            def project_out(i):
                if i == 1:
                    pe.wait_ge(av_ev, NH // 2)
                    pe.wait_ge(conv_ev, len(CONV_OUT))
                if i >= 2:
                    pe.wait_ge(mixg_done, 2 * (i - 1))
                for n in range(2):
                    for k in range(KC):
                        ins = t.matmul(ps[:, 4 + 2 * (i % 2) + n], mixT[:, k, i * P:(i + 1) * P],
                                       wo[:, k, n * 512:(n + 1) * 512], start=k == 0, stop=k == KC - 1)
                    ins.then_inc(out_done, 1)

            def transpose_h2(i):
                pe.wait_ge(h2_done, i + 1)
                pe.wait_ge(row_ev, 8)
                if i > 0:
                    pe.wait_ge(h2t_ev, i)
                for k in range(KC):
                    ins = t.transpose(flat[:, k * P:(k + 1) * P], h2p[i % 2][:, k * P:(k + 1) * P], ident[:])
                ins.then_inc(h2t_done, 1)

            def route(i):
                pe.wait_ge(h2t_ev, i + 1)
                for k in range(KC):
                    ins = t.matmul(ps[:, 2, i * (NG + NE):(i + 1) * (NG + NE)], h2T[:, k], w_r[:, k],
                                   start=k == 0, stop=k == KC - 1)
                ins.then_inc(logit_done, 1)

            pe.wait_ge(ld_wo, 16)
            pe.wait_ge(ld_wr, 32)
            pe.wait_ge(av_ev, NH // 2)
            pe.wait_ge(conv_ev, len(CONV_OUT))
            project_out(0)
            project_out(1)
            transpose_h2(0)
            project_out(2)
            route(0)
            transpose_h2(1)
            project_out(3)
            route(1)
            for i in (2, 3):
                transpose_h2(i)
                route(i)

            pe.wait_ge(mb_done, 1)
            pe.wait_ge(mixg_done, 2 * TC)
            m2d = mb.rearrange("p c e -> p (c e)")
            t.matmul(ps[:, 5, 0:P], before[:], m2d, start=True, stop=False, skip_group_check=True)
            for c in range(1, TC):
                t.matmul(ps[:, 5, c * NE:P], ones_b[:], m2d[:, 0:(TC - c) * NE], start=False, stop=False, skip_group_check=True)
            for c in range(TC):
                ins = t.matmul(ps[:, 5, P:P + NE], ones_b[:], mb[:, c], start=False, stop=c == TC - 1, skip_group_check=True)
            ins.then_inc(pos_done, 1)

            def slot_table(n, to, cols):
                pe.wait_ge(hot_done, n)
                for c in range(8):
                    ins = t.matmul(to, rowhot[:, c], cols[:, c].rearrange("p s n -> p (s n)"), start=c == 0, stop=c == 7)
                ins.then_inc(tab_done, 1)

            slot_table(1, ps[:, 4, 0:3 * NPAIR], colhot)

            def expert_rows(u, sem_done):
                for k in range(KC):
                    ins = t.transpose(flat[:, k * P:(k + 1) * P], xg[u][:, k * P:(k + 1) * P], ident[:])
                ins.then_inc(sem_done, 1)

            def gate_up(e, u, slot, sem_done):
                for k in range(KC):
                    for a in range(2):
                        ins = t.matmul(ps[a * SLOTS:(a + 1) * SLOTS, 2 + e, 0:2 * P],
                                       xT[u][:, k, e * SLOTS:(e + 1) * SLOTS],
                                       w_gu[slot][e][:, :, k, a * P:(a + 1) * P], start=k == 0, stop=k == KC - 1)
                ins.then_inc(sem_done, 1)

            def down(e, slot, sem_done):
                for a in range(2):
                    for b in range(2):
                        ins = t.matmul(ps[b * SLOTS:(b + 1) * SLOTS, 6 + e, :], hidT[e][:, a * SLOTS:(a + 1) * SLOTS],
                                       w_dn[slot][e][:, a, b * 512:(b + 1) * 512], start=a == 0, stop=a == 1)
                ins.then_inc(sem_done, 1)

            def turn(y, e):
                pe.wait_ge(hid_done, y + 1)
                if not isinstance(y, int) or y >= 2:
                    pe.wait_ge(tr_ev, y - 1)
                t.transpose(ps[:, 4 + e, 0:P], hid[e][:], ident[:]).then_inc(tr_done, 1)

            def finish(y, e, u, i):
                pe.wait_ge(tr_ev, y + 1)
                pe.wait_ge(ld_dn[u][e], 16 * (i + 1))
                if not isinstance(y, int) or y >= 2:
                    pe.wait_ge(y_ev, y - 1)
                down(e, u, dn_done)

            def pair(i, u, first=False, last=False):
                j = RING * i + u
                pu, pi = ((u - 1) % RING, i - 1 if u == 0 else i)
                if not first:
                    turn(2 * j - 1, 1)
                pe.wait_ge(xe_ev, j + 1)
                pe.wait_ge(ld_gu[u][0], 32 * (i + 1))
                if not first:
                    pe.wait_ge(hid_done, 2 * j - 1)
                gate_up(0, u, u, gu_done)
                if first:
                    slot_table(2, ps[:, 5, OVT:OVT + 3 * NOVP], colhot_ov)
                else:
                    finish(2 * j - 1, 1, pu, pi)
                turn(2 * j, 0)
                pe.wait_ge(ld_gu[u][1], 32 * (i + 1))
                if not first:
                    pe.wait_ge(hid_done, 2 * j)
                gate_up(1, u, u, gu_done)
                if not last:
                    nu = (u + 1) % RING
                    pe.wait_ge(gathered[nu], 16 * ((i + 1 if nu == 0 else i) + 1))
                    pe.wait_ge(xe_ev, j + 1)
                    expert_rows(nu, xe_done)
                finish(2 * j, 0, u, i)

            pe.wait_ge(gathered[0], 16)
            expert_rows(0, xe_done)
            for u in range(RING):
                pair(0, u, first=u == 0)
            with pe.Fori(1, NPAIR // RING) as i:
                for u in range(RING):
                    pair(i, u)
            pair(NPAIR // RING, 0, last=True)
            turn(NE - 1, 1)
            finish(NE - 1, 1, 0, NPAIR // RING)

            pe.wait_ge(flag_ready, 1)
            more = pe.value_load(flag[0:1, 0:1], min_val=0, max_val=NOVB)
            with pe.If(more > 0):
                with pe.Fori(0, NOVP) as j:
                    pe.wait_ge(ov_gathered, 16 * (j + 1))
                    pe.wait_ge(y_ev, NE + 2 * j)
                    expert_rows(0, xe_done)
                    pe.wait_ge(xe_ev, NPAIR + j + 1)
                    pe.wait_ge(ov_ld, 96 * (j + 1))
                    for e in range(2):
                        gate_up(e, 0, 0, gu_done)
                        pe.wait_ge(hid_done, NE + 2 * j + e + 1)
                        t.transpose(ps[:, 4 + e, 0:P], hid[e][:], ident[:]).then_inc(tr_done, 1)
                        pe.wait_ge(tr_ev, NE + 2 * j + e + 1)
                        down(e, 0, dn_done)


_INS = ["x", "c", "w_ada", "b_ada", "w_in", "conv_w", "w_out", "ln1_g", "ln1_b", "w_router_group",
        "b_router_group", "w_router_expert", "b_router_expert", "w_gate", "w_up", "w_down", "ln2_g", "ln2_b"]
_OUTS = [((1, T, D), "float32")]


def kernel(**inputs):
    import numpy as _np
    import concourse.bacc as _bacc
    from concourse import mybir as _mybir
    from concourse.bass_utils import run_bass_kernel_spmd as _run

    nc = _bacc.Bacc("TRN2", target_bir_lowering=False, num_devices=1)
    arrays, args = {}, []
    for name in _INS:
        a = _np.ascontiguousarray(inputs[name])
        arrays[f"in_{name}_dram"] = a
        args.append(nc.dram_tensor(f"in_{name}_dram", a.shape, _mybir.dt.from_np(a.dtype), kind="ExternalInput").ap())
    for i, (shape, dtype) in enumerate(_OUTS):
        dt = _mybir.dt.from_np(_np.dtype(dtype))
        args.append(nc.dram_tensor(f"out_{i}_dram", shape, dt, kind="ExternalOutput").ap())
    layer_kernel(nc, *args)
    r = _run(nc, [arrays], core_ids=[0])
    return tuple(r.results[0][f"out_{i}_dram"] for i in range(len(_OUTS)))[0]
```
